# Optimizing a Trainium2 kernel written in Bass

```python
import jax, jax.numpy as jnp
from jax import lax
import numpy as np

D_MODEL = 1024
BATCH = 1
SEQ = 1024
DEPTH = 2
DEC_BATCH = 1
DEC_SEQ = 32
PAST_LEN = 512

CHUNK = 64
Q_BLOCK = 128
D_HEAD = 64
H_A = (D_MODEL // 2) // D_HEAD
B_WIDTH = D_MODEL // 2
G_B = 4
B_CHUNK = 128
H_C = (D_MODEL // 2) // D_HEAD
KV_C = max(1, H_C // 4)
H_IDX = 4
D_IDX = 64
TOPK_MAX = 256
D_D = D_MODEL // 2
CONV_W = 3
D_FF = 4 * D_MODEL
N_EVEN = (DEPTH + 1) // 2
N_ODD = DEPTH // 2
EPS = 1e-6
NEG = -1e30
EVEN_SPLITS = (H_A * D_HEAD, H_A * D_HEAD, H_A * D_HEAD, B_WIDTH, B_WIDTH)
ODD_SPLITS = (H_C * D_HEAD, KV_C * D_HEAD, KV_C * D_HEAD, H_IDX * D_IDX, D_IDX, H_IDX, D_D, D_D, D_D)
EVEN_IN = sum(EVEN_SPLITS)
ODD_IN = sum(ODD_SPLITS)
MIX_OUT = H_A * D_HEAD + B_WIDTH

kernel_name = 'hybrid_streaming_encoder_step'

def rms_norm(x, g):
    xf = x.astype(jnp.float32)
    y = xf * lax.rsqrt(jnp.mean(xf * xf, axis=-1, keepdims=True) + EPS)
    return (y * g.astype(jnp.float32)).astype(x.dtype)

def split_cols(z, sizes):
    offs = np.cumsum((0,) + tuple(sizes))
    return [z[..., int(offs[i]):int(offs[i + 1])] for i in range(len(sizes))]

def to_blocks(a):
    b, s = a.shape[:2]
    return jnp.moveaxis(a.reshape((b, s // Q_BLOCK, Q_BLOCK) + a.shape[2:]), 1, 0)

def from_blocks(a):
    nb, b, qb = a.shape[:3]
    return jnp.moveaxis(a, 0, 1).reshape((b, nb * qb) + a.shape[3:])

def stick_breaking(q, k, v, q_pos, k_pos):
    f32 = jnp.float32
    z = jnp.einsum('bqhd,bkhd->bhqk', q.astype(f32), k.astype(f32)) * (D_HEAD ** -0.5)
    mask = k_pos[None, :] < q_pos[:, None]
    log_stay = jnp.where(mask, jax.nn.log_sigmoid(-z), 0.0)
    csum = jnp.cumsum(log_stay, axis=-1)
    after = csum[..., -1:] - csum
    w = jnp.where(mask, jnp.exp(jax.nn.log_sigmoid(z) + after), 0.0)
    return jnp.einsum('bhqk,bkhd->bqhd', w.astype(v.dtype), v)

def dsa_attend(q, qi, wi, q_pos, k, v, ki, k_pos, top_k):
    f32 = jnp.float32
    qk_idx = jnp.einsum('bqhe,bke->bqhk', qi.astype(f32), ki.astype(f32)) * (D_IDX ** -0.5)
    score = jnp.einsum('bqhk,bqh->bqk', jax.nn.relu(qk_idx), wi.astype(f32)) * (H_IDX ** -0.5)
    admissible = (k_pos[None, :] // CHUNK) <= (q_pos[:, None] // CHUNK)
    score = jnp.where(admissible, score, NEG)
    _, idx = lax.top_k(score, top_k)
    gather = jax.vmap(lambda rows, ii: rows[ii])
    k_sel = gather(k, idx)
    v_sel = gather(v, idx)
    sel_ok = (k_pos[idx] // CHUNK) <= (q_pos[None, :, None] // CHUNK)
    b_, nq = q.shape[:2]
    qg = q.reshape(b_, nq, KV_C, H_C // KV_C, D_HEAD)
    logits = jnp.einsum('bqgrd,bqkgd->bqgrk', qg.astype(f32), k_sel.astype(f32)) * (D_HEAD ** -0.5)
    logits = jnp.where(sel_ok[:, :, None, None, :], logits, NEG)
    p = jax.nn.softmax(logits, axis=-1)
    out = jnp.einsum('bqgrk,bqkgd->bqgrd', p.astype(v.dtype), v_sel)
    return out.reshape(b_, nq, H_C, D_HEAD)

def spatial_gate(u, vb, ws, bs, fresh_partial):
    pos = jnp.arange(B_CHUNK)
    causal = (pos[None, :] // CHUNK) <= (pos[:, None] // CHUNK)
    w = ws * causal.astype(ws.dtype)
    b_, t = vb.shape[:2]
    cg = B_WIDTH // G_B
    if fresh_partial:
        vr = vb.reshape(b_, 1, t, G_B, cg)
        w = w[:, :t, :t]
        bias = bs[:, :t]
    else:
        vr = vb.reshape(b_, t // B_CHUNK, B_CHUNK, G_B, cg)
        bias = bs
    mixed = jnp.einsum('gpq,bnqgc->bnpgc', w, vr) + bias.T[:, :, None]
    return u * mixed.reshape(b_, t, B_WIDTH)

def short_conv(cin, conv_w, prev):
    b_, t = cin.shape[:2]
    if prev is None:
        prev = jnp.zeros((b_, CONV_W - 1, D_D), cin.dtype)
    padded = jnp.concatenate([prev, cin], axis=1)
    y = conv_w[0] * padded[:, 0:t]
    for j in range(1, CONV_W):
        y = y + conv_w[j] * padded[:, j:j + t]
    return y, padded[:, t:]

def even_mixer(h, w_in, gq, gk, gb, ws, bs, w_out, past_k=None, past_v=None):
    b_, t = h.shape[:2]
    q, k, v, u, vb = split_cols(h @ w_in, EVEN_SPLITS)
    q = rms_norm(q.reshape(b_, t, H_A, D_HEAD), gq)
    k = rms_norm(k.reshape(b_, t, H_A, D_HEAD), gk)
    v = v.reshape(b_, t, H_A, D_HEAD)
    if past_k is None:
        pos = jnp.arange(t)
        att = from_blocks(lax.map(lambda a: stick_breaking(a[0], k, v, a[1], pos),
                                  (to_blocks(q), pos.reshape(-1, Q_BLOCK))))
    else:
        p = past_k.shape[1]
        att = stick_breaking(q, jnp.concatenate([past_k, k], axis=1),
                             jnp.concatenate([past_v, v], axis=1),
                             p + jnp.arange(t), jnp.arange(p + t))
    u = jax.nn.gelu(u)
    vb = rms_norm(jax.nn.gelu(vb), gb)
    gated = spatial_gate(u, vb, ws, bs, past_k is not None)
    out = jnp.concatenate([att.reshape(b_, t, -1), gated], axis=-1) @ w_out
    return out, k, v, vb

def odd_mixer(h, w_in, gq, gk, conv_w, w_out, past_k=None, past_v=None, past_ki=None, past_conv=None):
    b_, t = h.shape[:2]
    q, k, v, qi, ki, wi, gate_b, gate_c, hd = split_cols(h @ w_in, ODD_SPLITS)
    q = rms_norm(q.reshape(b_, t, H_C, D_HEAD), gq)
    k = rms_norm(k.reshape(b_, t, KV_C, D_HEAD), gk)
    v = v.reshape(b_, t, KV_C, D_HEAD)
    qi = qi.reshape(b_, t, H_IDX, D_IDX)
    if past_k is None:
        pos = jnp.arange(t)
        top_k = min(TOPK_MAX, t // 4)
        att = from_blocks(lax.map(lambda a: dsa_attend(a[0], a[1], a[2], a[3], k, v, ki, pos, top_k),
                                  (to_blocks(q), to_blocks(qi), to_blocks(wi), pos.reshape(-1, Q_BLOCK))))
    else:
        p = past_k.shape[1]
        top_k = min(TOPK_MAX, (p + t) // 4)
        att = dsa_attend(q, qi, wi, p + jnp.arange(t),
                         jnp.concatenate([past_k, k], axis=1),
                         jnp.concatenate([past_v, v], axis=1),
                         jnp.concatenate([past_ki, ki], axis=1),
                         jnp.arange(p + t), top_k)
    conv, new_conv = short_conv(gate_c * hd, conv_w, past_conv)
    out = jnp.concatenate([att.reshape(b_, t, -1), gate_b * conv], axis=-1) @ w_out
    return out, k, v, ki, new_conv

def sq_relu_ffn(h, w1, w2):
    return jnp.square(jax.nn.relu(h @ w1)) @ w2

def setup_inputs(seed: int = 0) -> dict:
    key = jax.random.key(seed)
    ks = iter(jax.random.split(key, 32))

    def nrm(shape, scale=1.0):
        return jax.random.normal(next(ks), shape, jnp.float32) * scale

    def gain(shape):
        return 1.0 + 0.05 * nrm(shape)

    return {
        'x_prompt': nrm((BATCH, SEQ, D_MODEL)),
        'x_sample': nrm((DEC_BATCH, DEC_SEQ, D_MODEL)),
        'cache_a_k': nrm((N_EVEN, DEC_BATCH, PAST_LEN, H_A, D_HEAD)),
        'cache_a_v': nrm((N_EVEN, DEC_BATCH, PAST_LEN, H_A, D_HEAD)),
        'cache_c_k': nrm((N_ODD, DEC_BATCH, PAST_LEN, KV_C, D_HEAD)),
        'cache_c_v': nrm((N_ODD, DEC_BATCH, PAST_LEN, KV_C, D_HEAD)),
        'cache_c_kidx': nrm((N_ODD, DEC_BATCH, PAST_LEN, D_IDX)),
        'state_d_conv': nrm((N_ODD, DEC_BATCH, CONV_W - 1, D_D)),
        'norm_mix_g': gain((DEPTH, D_MODEL)),
        'norm_ffn_g': gain((DEPTH, D_MODEL)),
        'w_in_even': nrm((N_EVEN, D_MODEL, EVEN_IN), D_MODEL ** -0.5),
        'gq_a': gain((N_EVEN, D_HEAD)),
        'gk_a': gain((N_EVEN, D_HEAD)),
        'g_b': gain((N_EVEN, B_WIDTH)),
        'ws_b': nrm((N_EVEN, G_B, B_CHUNK, B_CHUNK), B_CHUNK ** -0.5),
        'bs_b': gain((N_EVEN, G_B, B_CHUNK)),
        'w_out_even': nrm((N_EVEN, MIX_OUT, D_MODEL), MIX_OUT ** -0.5),
        'w_in_odd': nrm((N_ODD, D_MODEL, ODD_IN), D_MODEL ** -0.5),
        'gq_c': gain((N_ODD, D_HEAD)),
        'gk_c': gain((N_ODD, D_HEAD)),
        'conv_w_d': nrm((N_ODD, CONV_W, D_D), CONV_W ** -0.5),
        'w_out_odd': nrm((N_ODD, MIX_OUT, D_MODEL), MIX_OUT ** -0.5),
        'w_ffn1': nrm((DEPTH, D_MODEL, D_FF), D_MODEL ** -0.5),
        'w_ffn2': nrm((DEPTH, D_FF, D_MODEL), D_FF ** -0.5),
    }

def reference(x_prompt, x_sample, cache_a_k, cache_a_v, cache_c_k, cache_c_v, cache_c_kidx, state_d_conv,
              norm_mix_g, norm_ffn_g, w_in_even, gq_a, gk_a, g_b, ws_b, bs_b, w_out_even,
              w_in_odd, gq_c, gk_c, conv_w_d, w_out_odd, w_ffn1, w_ffn2):
    xp, xs = x_prompt, x_sample
    ak_p, av_p, ak_s, av_s, bv_s = [], [], [], [], []
    ck_p, cv_p, ci_p, ck_s, cv_s, ci_s, dc_p, dc_s = [], [], [], [], [], [], [], []
    for i in range(DEPTH):
        j = i // 2
        hp = rms_norm(xp, norm_mix_g[i])
        hs = rms_norm(xs, norm_mix_g[i])
        if i % 2 == 0:
            lw = (w_in_even[j], gq_a[j], gk_a[j], g_b[j], ws_b[j], bs_b[j], w_out_even[j])
            mp, kp, vp, _ = even_mixer(hp, *lw)
            ms, ks_, vs_, vbs = even_mixer(hs, *lw, past_k=cache_a_k[j], past_v=cache_a_v[j])
            ak_p.append(kp); av_p.append(vp)
            ak_s.append(ks_); av_s.append(vs_); bv_s.append(vbs)
        else:
            lw = (w_in_odd[j], gq_c[j], gk_c[j], conv_w_d[j], w_out_odd[j])
            mp, kp, vp, kip, cvp = odd_mixer(hp, *lw)
            ms, ks_, vs_, kis, cvs = odd_mixer(hs, *lw, past_k=cache_c_k[j], past_v=cache_c_v[j],
                                               past_ki=cache_c_kidx[j], past_conv=state_d_conv[j])
            ck_p.append(kp); cv_p.append(vp); ci_p.append(kip); dc_p.append(cvp)
            ck_s.append(ks_); cv_s.append(vs_); ci_s.append(kis); dc_s.append(cvs)
        xp = xp + mp
        xs = xs + ms
        xp = xp + sq_relu_ffn(rms_norm(xp, norm_ffn_g[i]), w_ffn1[i], w_ffn2[i])
        xs = xs + sq_relu_ffn(rms_norm(xs, norm_ffn_g[i]), w_ffn1[i], w_ffn2[i])
    return (xp, xs,
            jnp.stack(ak_p), jnp.stack(av_p), jnp.stack(ak_s), jnp.stack(av_s),
            jnp.stack(bv_s),
            jnp.stack(ck_p), jnp.stack(cv_p), jnp.stack(ci_p),
            jnp.stack(ck_s), jnp.stack(cv_s), jnp.stack(ci_s),
            jnp.stack(dc_p), jnp.stack(dc_s))


_drawn_inputs = setup_inputs


def setup_inputs(seed=0):
    import zlib

    import numpy as np

    out = dict(_drawn_inputs(seed))
    spreads = {}
    factors = {'gq_a': 4.208, 'gq_c': 8.0}
    for name, (base, spread) in spreads.items():
        noise = np.random.default_rng([zlib.crc32(name.encode()), seed]).standard_normal(out[name].shape)
        drawn = base * np.exp(spread * noise) if base else spread * noise
        out[name] = __import__('jax').numpy.asarray(drawn.astype(out[name].dtype))
    for name, factor in factors.items():
        out[name] = (out[name] * factor).astype(out[name].dtype)
    return out
```

```python
from contextlib import ExitStack

import concourse.bass as bass
from concourse import mybir

F32 = mybir.dt.float32
F32R = mybir.dt.float32r
U32 = mybir.dt.uint32
I32 = mybir.dt.int32
ALU = mybir.AluOpType
ACT = mybir.ActivationFunctionType

P = 128
D = 1024
KT = D // P
TP, TS = 1024, 32
NT = TP + TS
NTT = 9
NCH, CH = 3, NT // 3
FF = 4096
PAST = 512
PT = PAST // P
HD = 64
NH = 8
EPS = 1e-6
NEG = -1e30
BIG = 1e30
QC = 512
UN = 2048
EVEN_IN = 2560
ODD_IN = 2628
EQ, EK, EV, EU, EVB = 0, 4, 8, 12, 16
OQ, OK, OV, OQI, OKI, OB, OC, OH = 0, 4, 5, 6, 8, 9, 13, 17
NZ = 21
ODD_UNITS = [(768, 256), (1024, 68), (0, 256), (256, 256), (512, 256),
             (1092, 256), (1348, 256), (1604, 256), (1860, 256), (2116, 256), (2372, 256)]
U_EIN, U_EOUT, U_F0, U_OIN, U_OOUT, U_F1, U_END = 0, 10, 14, 46, 57, 61, 93
J_N0 = 0
J_EIN = 1
J_EN = 21
J_EOUT = 30
J_N1 = 38
J_F0 = 39
J_N2 = 199
J_OI = 200
J_OIN = 203
J_ON = 221
J_OOUT = 226
J_N3 = 234
J_F1 = 235
NCHUNK = FF // 256
TOPK = 256
TOPK_S = (PAST + TS) // 4
SCORE0 = [0, 0, 0] + [sum(P * (b + 1) for b in range(2, n)) for n in range(3, 9)]
SC_S = sum(P * (b + 1) for b in range(2, 8))


def tok(i):
    return i * P, (P if i < 8 else TS)


def build_encoder(nc, dram):
    ctx = ExitStack()
    with ctx:
        base = (nc.sbuf_base + 31) // 32 * 32

        def at(name, offset, shape, dtype=F32):
            return nc.alloc_sbuf_tensor_at(name, shape, dtype, offset=base + offset)

        def sem(name):
            return ctx.enter_context(nc.semaphore(name))

        ZB = NT * 4
        o_z = 0
        o_h = o_z + NZ * ZB
        o_w = o_h + 2 * KT * ZB
        o_e = o_w + 6 * UN * 4
        o_f = o_e + (SC_S + PAST + TS) * 4
        Z = at("Z", o_z, [P, NZ, NT])
        xT = at("xT", o_z, [P, KT, NT])
        hid = at("hid", o_z + KT * ZB, [P, 2, 2, 2, NT], F32R)
        hnf = at("hnf", o_z + KT * ZB, [P, 2, NT])
        rbuf = at("rbuf", o_z + 16 * ZB, [P, 2, NT])
        h = at("h", o_h, [P, KT, 2, NT], F32R)
        sq = at("sq", o_h, [P, 16, NT])
        sqx = at("sqx", o_z + 10 * ZB, [P, KT, NT])
        stage = at("stage", o_w, [P, 2, UN])
        w_sp = at("w_sp", o_w + 2 * UN * 4, [P, 2, 2, UN], F32R)
        xtok = at("xtok", o_h, [P, NTT, D])
        rstd = at("rstd", o_e, [P, NT])
        ident = at("ident", o_f, [P, P])
        ones = at("ones", o_f + 512, [P, P])
        blk = at("blk", o_f + 1024, [P, P])
        gv = at("gv", o_f + 1536, [P, 64])
        eps = at("eps", o_f + 1792, [P, 1])
        wi = at("wi", o_f + 1824, [P, NTT, 4])
        bs_ = at("bs_", o_f + 1984, [P, 10, 8])
        G_MIX, G_FFN, G_QA, G_KA, G_VB, G_QC, G_KC, G_CW = 0, 16, 32, 33, 34, 38, 39, 40
        vtok = at("vtok", o_h, [P, NTT, 512])
        vbtok = at("vbtok", o_h + 18432, [P, NTT, 512])
        ktok = at("ktok", o_z + 16 * ZB, [P, NTT, 512])
        abuf = at("abuf", o_h + 18432, [P, 9, QC])
        abuf2 = at("abuf2", o_h + 61440, [P, 3, QC])
        zs = [abuf[:, i, :] for i in range(4)]
        sp = [abuf[:, 4 + i, :] for i in range(3)]
        lb = [abuf[:, 7 + i, :] for i in range(2)]
        wb = [abuf2[:, i, :] for i in range(3)]
        kpt = at("kpt", o_h + 36864, [P, PT, 512])
        kpT = at("kpT", o_h + 45056, [P, 4, PAST])
        vpt = at("vpt", o_h + 53248, [P, PT, 512])
        tri = at("tri", o_e + 4224, [P, P])
        ctri = at("ctri", o_e + 4736, [P, P])
        dneg = at("dneg", o_e + 5248, [P, P])
        wsb = at("wsb", o_e + 5760, [P, 4, P])
        wsT = at("wsT", o_e + 7808, [P, 4, P])
        bsr = at("bsr", o_e + 9856, [1, 512])
        score = at("score", o_e, [P, SC_S + PAST + TS])
        PS = ctx.enter_context(nc.psum_tensor("PS", [P, 8, 512], F32))

        def psz(j):
            s = 3 * (j % 2)
            return PS[:, s:s + 3, 0:CH]

        def tri3(a):
            return a.rearrange("p (c n) -> p c n", c=NCH)

        spill = nc.dram_tensor("x_spill", [P, KT * NT], F32).ap()

        w_stage = [sem("w_stage0"), sem("w_stage1")]
        w_hi_done = sem("w_hi_done")
        w_split = sem("w_split")
        job_done = sem("job_done")
        set_free = [sem("set_free0"), sem("set_free1")]
        consts = sem("consts")
        vecs = sem("vecs")
        x_in = [sem(f"x_in{i}") for i in range(NTT)]
        x_tp = sem("x_tp")
        xT_ready = sem("xT_ready")
        sq_done = sem("sq_done")
        rt_done = sem("rt_done")
        rs_done = sem("rs_done")
        hf_done = sem("hf_done")
        hi_done = sem("hi_done")
        h_ready = sem("h_ready")
        spilled = sem("spilled")
        x_back = sem("x_back")
        z_done = sem("z_done")
        o_added = sem("o_added")
        r_done = sem("r_done")
        s_done = sem("s_done")
        hhi_done = sem("hhi_done")
        hid_ready = sem("hid_ready")
        out_dma = sem("out_dma")
        act_step = sem("act_step")
        dve_step = sem("dve_step")
        pool_step = sem("pool_step")
        outs = [0]

        class Chain:

            def __init__(self, eng, s):
                self.eng, self.s, self.n, self.loop = eng, s, 0, 0

            def link(self, ins):
                self.n += 1
                ins.then_inc(self.s, 1)
                self.eng.wait_ge(self.s, self.n + self.loop)

            def begin(self, i, per):
                self.loop, self.first, self.per = i * per, self.n, per

            def end(self, times):
                assert self.n == self.first + self.per
                self.n, self.loop = self.first + self.per * times, 0

        def evacuated(eng, j, dj2=0):
            eng.wait_ge(set_free[j % 2], j // 2 + 1 + dj2)

        def out_start(eng, dst, src, **kw):
            eng.dma_start(dst, src, **kw).then_inc(out_dma, 16)
            outs[0] += 1

        def gemm_tile(pe, j, slot, nk, wcol, wstep, m, rhs, dj2=0):
            pe.wait_ge(set_free[j % 2], j // 2 + dj2)
            out = psz(j)
            for k in range(nk):
                for n, (a, b) in enumerate(((0, 0), (0, 1), (1, 0))):
                    lhs = w_sp[:, slot, a, k * wstep + wcol:k * wstep + wcol + m]
                    for c in range(NCH):
                        mm = pe.matmul(out[0:m, c, :], lhs, rhs(k, b)[:, c * CH:(c + 1) * CH],
                                       start=(k == 0 and n == 0), stop=(k == nk - 1 and n == 2))
            mm.then_inc(job_done, 1)

        def gemm_in_unit(pe, u, j, widths=(P, P), du=0, dj2=0):
            pe.wait_ge(w_split, u + 1 + du)
            for t, m in enumerate(widths):
                gemm_tile(pe, j + t, u % 2, KT, t * P, 256, m, lambda k, b: h[:, k, b, :], dj2)

        def pe_ffn(pe, u0, j0, blkh, c0):
            pe.wait_ge(h_ready, 8 * (blkh + 1))
            gemm_in_unit(pe, u0, j0)

            def chunk(c, first_up=True, du=0, dj2=0, dh=0):
                u, j = u0 + 2 * c + 1, j0 + 2 + 10 * c
                if first_up:
                    gemm_in_unit(pe, u, j, du=du, dj2=dj2)
                    u, j = u + 1, j + 2
                pe.wait_ge(w_split, u + 1 + du)
                pe.wait_ge(hid_ready, c0 + 2 * c + 2 + dh)
                for m in range(KT):
                    gemm_tile(pe, j + m, u % 2, 2, m * P, D, P, lambda k, b: hid[:, c % 2, k, b, :], dj2)

            with pe.Fori(0, 7) as i:
                for c in range(2):
                    chunk(c, du=i * 4, dj2=i * 10, dh=i * 4)
            chunk(14)
            chunk(15, first_up=False)

        def act_ffn(act, ch, j0, c0):
            def up(c, dj2=0, dj=0, dt=0):
                j = j0 if c == 0 else j0 + 2 + 10 * (c - 1)
                for t in range(2):
                    n = c0 + 2 * c + t
                    act.wait_ge(job_done, j + t + 1 + dj)
                    if n >= 2:
                        act.wait_ge(hid_ready, n - 1 + dt)
                    act.activation(tri3(rbuf[:, t, :]), psz(j + t), ACT.Relu).then_inc(set_free[(j + t) % 2], 1)
                    act.wait_ge(s_done, n + 1 + dt)
                    act.activation(hid[:, c % 2, t, 0, :], rbuf[:, t, :], ACT.Copy).then_inc(hhi_done, 1)

            up(0)
            with act.Fori(0, 7) as i:
                for c in (1, 2):
                    up(c, dj2=i * 10, dj=i * 20, dt=i * 4)
            up(15)

        def dve_ffn(dve, ch, j0, c0):
            def up(c, dj2=0, dj=0, dt=0):
                j = j0 if c == 0 else j0 + 2 + 10 * (c - 1)
                for t in range(2):
                    n = c0 + 2 * c + t
                    evacuated(dve, j + t, dj2)
                    dve.tensor_tensor(rbuf[:, t, :], rbuf[:, t, :], rbuf[:, t, :], ALU.mult).then_inc(s_done, 1)
                    dve.wait_ge(hhi_done, n + 1 + dt)
                    dve.tensor_tensor(hid[:, c % 2, t, 1, :], rbuf[:, t, :], hid[:, c % 2, t, 0, :].bitcast(F32),
                                      ALU.subtract).then_inc(hid_ready, 1)

            def down(c, dj2=0, dj=0):
                j = j0 + 2 + 10 * c + (2 if c < 15 else 0)
                for m in range(KT):
                    dve.wait_ge(job_done, j + m + 1 + dj)
                    dve.tensor_tensor(tri3(xT[:, m, :]), psz(j + m), tri3(xT[:, m, :]),
                                      ALU.add).then_inc(set_free[(j + m) % 2], 1)

            up(0)
            with dve.Fori(0, 7) as i:
                for c in (0, 1):
                    up(c + 1, dj2=i * 10, dj=i * 20, dt=i * 4)
                    down(c, dj2=i * 10, dj=i * 20)
            up(15)
            down(14)
            down(15)

        def x_tile_ready(eng, n, m):
            if n == 0:
                eng.wait_ge(xT_ready, NTT)
            else:
                evacuated(eng, {1: J_EOUT, 2: J_F0 + 152, 3: J_OOUT, 4: J_F1 + 152}[n] + m)

        NBLK = [0, 2, 3, 5]
        NJOB = [J_N0, J_N1, J_N2, J_N3]

        def sq_of(n):
            return sqx if n % 2 else sq

        def act_norm(act, n):
            for k in range(KT):
                x_tile_ready(act, n, k)
                act.activation(sq_of(n)[:, k, :], xT[:, k, :], ACT.Square).then_inc(sq_done, 1)
            if n in (0, 2):
                act.dma_start(spill, xT[:, :, :].rearrange("p k n -> p (k n)")).then_inc(spilled, 16)
            j = NJOB[n]
            act.wait_ge(job_done, j + 1)
            act.activation(tri3(rstd[:, :]), psz(j), ACT.Sqrt, bias=eps[:, 0:1],
                           scale=1.0 / D).then_inc(set_free[j % 2], 1)
            for k in range(KT):
                act.wait_ge(hf_done, 8 * n + k + 1)
                act.activation(h[:, k, 0, :], hnf[:, k % 2, :], ACT.Copy).then_inc(hi_done, 1)

        def pe_norm(pe, n):
            j = NJOB[n]
            if j >= 2:
                pe.wait_ge(set_free[j % 2], j // 2)
            for k in range(KT):
                pe.wait_ge(sq_done, 8 * n + k + 1)
                for c in range(NCH):
                    mm = pe.matmul(psz(j)[:, c, :], ones[:, :], sq_of(n)[:, k, c * CH:(c + 1) * CH],
                                   start=(k == 0), stop=(k == KT - 1))
            mm.then_inc(job_done, 1)

        def dve_norm(dve, ch, n):
            evacuated(dve, NJOB[n])
            ch.link(dve.reciprocal(rstd[:, :], rstd[:, :]))
            g0 = [G_MIX, G_FFN, G_MIX + 8, G_FFN + 8][n]
            for k in range(KT):
                dve.scalar_tensor_tensor(hnf[:, k % 2, :], xT[:, k, :], gv[:, g0 + k:g0 + k + 1], rstd[:, :],
                                         ALU.mult, ALU.mult).then_inc(hf_done, 1)
                dve.wait_ge(hi_done, 8 * NBLK[n] + k + 1)
                dve.wait_ge(hf_done, 8 * n + k + 1)
                dve.tensor_tensor(h[:, k, 1, :], hnf[:, k % 2, :], h[:, k, 0, :].bitcast(F32),
                                  ALU.subtract).then_inc(h_ready, 1)

        def act_mix(act, b, slots, done, count, stored, bytes_):
            act.wait_ge(done, count)
            act.wait_ge(stored, bytes_)
            for k, s in enumerate(slots):
                act.activation(h[:, k, 0, :], Z[:, s, :], ACT.Copy).then_inc(hi_done, 1)
            act.wait_ge(h_ready, 8 * (b + 1))
            act.dma_start(xT[:, :, :].rearrange("p k n -> p (k n)"), spill).then_inc(x_back, 16)

        def dve_mix(dve, b, slots):
            for k, s in enumerate(slots):
                dve.wait_ge(hi_done, 8 * b + k + 1)
                dve.tensor_tensor(h[:, k, 1, :], Z[:, s, :], h[:, k, 0, :].bitcast(F32),
                                  ALU.subtract).then_inc(h_ready, 1)

        def pe_outproj(pe, u0, j0, b):
            pe.wait_ge(h_ready, 8 * (b + 1))
            with pe.Fori(0, 2) as i:
                for s in range(2):
                    gemm_in_unit(pe, u0 + s, j0 + 2 * s, du=i * 2, dj2=i * 2)

        def dve_outproj(dve, j0, times):
            dve.wait_ge(x_back, 16 * times)
            for m in range(KT):
                dve.wait_ge(job_done, j0 + m + 1)
                dve.tensor_tensor(tri3(xT[:, m, :]), psz(j0 + m), tri3(xT[:, m, :]),
                                  ALU.add).then_inc(set_free[(j0 + m) % 2], 1)

        E_NORMS = [(EVB, 4, ones, G_VB, 1.0 / 512)] + [(EQ + i, 1, blk, G_QA, 1.0 / HD) for i in range(4)] + \
                  [(EK + i, 1, blk, G_KA, 1.0 / HD) for i in range(4)]
        O_NORMS = [(OQ + i, 1, blk, G_QC, 1.0 / HD) for i in range(4)] + [(OK, 1, blk, G_KC, 1.0 / HD)]
        zsq = sem("zsq")
        zn = sem("zn")

        def act_znorm(act, norms, j0, q0, jlast):
            evacuated(act, jlast - 1)
            evacuated(act, jlast - 2)
            n = 0
            for s, cnt, _, _, _ in norms:
                for i in range(cnt):
                    act.activation(sq[:, n, :], Z[:, s + i, :], ACT.Square).then_inc(zsq, 1)
                    n += 1
            n = 0
            for i, (s, cnt, _, _, scale) in enumerate(norms):
                act.wait_ge(job_done, j0 + i + 1)
                act.activation(tri3(sq[:, n, :]), psz(j0 + i), ACT.Sqrt, bias=eps[:, 0:1],
                               scale=scale).then_inc(set_free[(j0 + i) % 2], 1)
                n += cnt

        def pe_znorm(pe, norms, j0, q0):
            n = 0
            for i, (s, cnt, w, _, _) in enumerate(norms):
                j = j0 + i
                pe.wait_ge(set_free[j % 2], j // 2)
                for t in range(cnt):
                    pe.wait_ge(zsq, q0 + n + 1)
                    for c in range(NCH):
                        mm = pe.matmul(psz(j)[:, c, :], w[:, :], sq[:, n, c * CH:(c + 1) * CH],
                                       start=(t == 0), stop=(t == cnt - 1))
                    n += 1
                mm.then_inc(job_done, 1)

        def dve_znorm(dve, ch, norms, j0):
            n = 0
            for i, (s, cnt, _, g, _) in enumerate(norms):
                evacuated(dve, j0 + i)
                ch.link(dve.reciprocal(sq[:, n, :], sq[:, n, :]))
                for t in range(cnt):
                    gc = g + (t if cnt > 1 else 0)
                    dve.scalar_tensor_tensor(Z[:, s + t, :], Z[:, s + t, :], gv[:, gc:gc + 1], sq[:, n, :],
                                             ALU.mult, ALU.mult).then_inc(zn, 1)
                n += cnt

        turned = sem("turned")
        turn_rd = [sem("turn_dve"), sem("turn_act")]
        E_TURNS = [(s, x, i) for s, x in ((EVB, vbtok), (EV, vtok), (EK, ktok)) for i in range(NTT)]

        def pe_even_turns(pe):
            pe.wait_ge(zn, 12)
            for n, (s, x, i) in enumerate(E_TURNS):
                c0, m = tok(i)
                if n >= 8:
                    pe.wait_ge(turn_rd[n % 2], (n - 8) // 2 + 1)
                for t in range(4):
                    mm = pe.transpose(PS[0:m, n % 8, t * P:(t + 1) * P], Z[:, s + t, c0:c0 + m], ident[:, :])
                mm.then_inc(turned, 1)

        def read_even_turns(eng, par):
            for n, (s, x, i) in enumerate(E_TURNS):
                if n % 2 == par:
                    _, m = tok(i)
                    eng.wait_ge(turned, n + 1)
                    if x is ktok:
                        eng.wait_ge(turned, 18)
                    if par == 0:
                        ins = eng.tensor_copy(x[0:m, i, :], PS[0:m, n % 8, :])
                    else:
                        ins = eng.activation(x[0:m, i, :], PS[0:m, n % 8, :], ACT.Copy)
                    ins.then_inc(turn_rd[par], 1)

        ws_in = sem("ws_in")
        ws_t = sem("ws_t")
        ws_rd = sem("ws_rd")
        sg_done = sem("sg_done")
        sg_rd = sem("sg_rd")

        def pe_spatial(pe):
            pe.wait_ge(ws_in, 32)
            pe.wait_ge(turn_rd[0], 14)
            pe.wait_ge(turn_rd[1], 13)
            for g in range(4):
                mm = pe.transpose(PS[:, 7, g * P:(g + 1) * P], wsb[:, g, :], ident[:, :])
            mm.then_inc(ws_t, 1)
            pe.wait_ge(ws_rd, 2)
            for i in range(NTT):
                c0, m = tok(i)
                if i >= 4:
                    pe.wait_ge(sg_rd, i - 3)
                out = PS[:, i % 4, :].rearrange("p (g q) -> p g q", g=4)
                pe.matmul(out[:, :, 0:m], ones[0:1, :], bsr[:, :].rearrange("p (g q) -> p g q", g=4)[:, :, 0:m],
                          start=True, stop=False, skip_group_check=True)
                for g in range(4):
                    mm = pe.matmul(out[:, g, 0:m], vbtok[0:m, i, g * P:(g + 1) * P], wsT[0:m, g, 0:m],
                                   start=False, stop=True, skip_group_check=True)
                mm.then_inc(sg_done, 1)

        def dve_spatial(dve, ch):
            dve.wait_ge(ws_t, 1)
            dve.tensor_copy(wsT[:, :, :], PS[:, 7, :].rearrange("p (g q) -> p g q", g=4)).then_inc(ws_rd, 1)
            dve.wait_ge(ws_rd, 1)
            dve.memset(wsT[64:128, :, 0:64], 0.0).then_inc(ws_rd, 1)
            for i in range(NTT):
                c0, m = tok(i)
                dve.wait_ge(sg_done, i + 1)
                u = Z[:, EU:EU + 4, c0:c0 + m]
                dve.tensor_tensor(u, PS[:, i % 4, :].rearrange("p (g q) -> p g q", g=4)[:, :, 0:m], u,
                                  ALU.mult).then_inc(sg_rd, 1)

        STEPS = []
        for p_ in range(4):
            for qc_ in range(2):
                for kt_ in range(4 * qc_ + 3, -1, -1):
                    for e_ in range(2):
                        STEPS.append((p_, qc_, kt_, e_))
        NS = len(STEPS)
        a_z = sem("a_z")
        a_na = sem("a_na")
        a_l = sem("a_l")
        a_sp = sem("a_sp")
        a_s = sem("a_s")
        a_t = sem("a_t")
        a_w = sem("a_w")
        a_pv = sem("a_pv")
        a_o = sem("a_o")

        def span(s):
            p, qc, kt, e = STEPS[s]
            return max(0, kt * P - qc * QC)

        def group_of(s):
            return 2 * STEPS[s][0] + STEPS[s][1]

        def first(s):
            return STEPS[s][2] == 4 * STEPS[s][1] + 3

        def last(s):
            return STEPS[s][2] == 0

        def pe_stick(pe):
            pe.wait_ge(sg_rd, NTT)
            for it in range(NS + 3):
                if it < NS:
                    p, qc, kt, e = STEPS[it]
                    if it >= 3:
                        pe.wait_ge(a_na, it - 2)
                    c0 = span(it)
                    pe.matmul(PS[:, it % 3, c0:QC], Z[64 * e:64 * e + 64, EK + p, kt * P:(kt + 1) * P],
                              Z[64 * e:64 * e + 64, EQ + p, qc * QC + c0:(qc + 1) * QC],
                              start=True, stop=True).then_inc(a_z, 1)
                s = it - 2
                if 0 <= s < NS:
                    p, qc, kt, e = STEPS[s]
                    pe.wait_ge(a_sp, s + 1)
                    if s >= 2:
                        pe.wait_ge(a_t, s - 1)
                    c0 = span(s)
                    pe.matmul(PS[:, 3 + e, c0:QC], tri[:, :], sp[s % 3][:, c0:QC], start=first(s), stop=True,
                              skip_group_check=True).then_inc(a_s, 1)
                s = it - 3
                if 0 <= s < NS:
                    p, qc, kt, e = STEPS[s]
                    g = group_of(s)
                    c0 = span(s)
                    pe.wait_ge(a_w, s + 1)
                    if first(s) and g >= 2:
                        pe.wait_ge(a_o, g - 1)
                    if not last(s):
                        pe.matmul(PS[:, 3 + e, c0:QC], ctri[:, :], sp[s % 3][:, c0:QC], start=False, stop=True,
                                  skip_group_check=True)
                    h0 = (2 * p + e) * HD
                    pe.matmul(PS[64 * e:64 * e + 64, 5 + g % 2, c0:QC], vtok[:, kt, h0:h0 + HD],
                              wb[s % 3][:, c0:QC], start=first(s), stop=last(s),
                              skip_group_check=True).then_inc(a_pv, 1)

        def dve_stick(dve, ch):
            for it in range(NS + 3):
                if it < NS:
                    p, qc, kt, e = STEPS[it]
                    c0 = span(it)
                    dve.wait_ge(a_z, it + 1)
                    z = zs[it % 4]
                    ch.link(dve.tensor_scalar(z[:, c0:QC], PS[:, it % 3, c0:QC], HD ** -0.5, None, ALU.mult))
                    if kt >= 4 * qc:
                        ch.link(dve.tensor_tensor(z[:, c0:c0 + P], z[:, c0:c0 + P], dneg[:, :], ALU.add))
                    dve.scalar_tensor_tensor(lb[it % 2][:, c0:QC], z[:, c0:QC], -1.0, z[:, c0:QC], ALU.mult,
                                             ALU.min).then_inc(a_na, 1)
                s = it - 1
                if 0 <= s < NS:
                    c0 = span(s)
                    dve.wait_ge(a_l, s + 1)
                    if s >= 3:
                        dve.wait_ge(a_pv, s - 2)
                    dve.scalar_tensor_tensor(sp[s % 3][:, c0:QC], zs[s % 4][:, c0:QC], 0.0, lb[s % 2][:, c0:QC],
                                             ALU.max, ALU.add).then_inc(a_sp, 1)
                s = it - 2
                if 0 <= s < NS:
                    c0 = span(s)
                    e = STEPS[s][3]
                    dve.wait_ge(a_s, s + 1)
                    if s >= 3:
                        dve.wait_ge(a_pv, s - 2)
                    dve.scalar_tensor_tensor(wb[s % 3][:, c0:QC], PS[:, 3 + e, c0:QC], -1.0,
                                             zs[s % 4][:, c0:QC], ALU.mult, ALU.add).then_inc(a_t, 1)
                s = it - 3
                if 0 <= s < NS and last(s) and STEPS[s][3] == 1:
                    p, qc, kt, e = STEPS[s]
                    g = group_of(s)
                    dve.wait_ge(a_pv, s + 1)
                    dve.tensor_copy(Z[:, EQ + p, qc * QC:(qc + 1) * QC], PS[:, 5 + g % 2, :]).then_inc(a_o, 1)

        def act_stick(act, ch):
            for it in range(NS + 3):
                if it < NS:
                    c0 = span(it)
                    act.wait_ge(a_na, it + 1)
                    x = lb[it % 2][:, c0:QC]
                    ch.link(act.activation(x, x, ACT.Exp))
                    act.activation(x, x, ACT.Ln, bias=1.0).then_inc(a_l, 1)
                s = it - 2
                if 0 <= s < NS:
                    c0 = span(s)
                    act.wait_ge(a_t, s + 1)
                    x = wb[s % 3][:, c0:QC]
                    act.activation(x, x, ACT.Exp).then_inc(a_w, 1)

        b_in = sem("b_in")
        b_kt = sem("b_kt")
        b_kr = sem("b_kr")
        b_z = sem("b_z")
        b_na = sem("b_na")
        b_l = sem("b_l")
        b_sp = sem("b_sp")
        b_s = sem("b_s")
        b_t = sem("b_t")
        b_w = sem("b_w")
        b_pv = sem("b_pv")
        att_a = sem("att_a")
        SW = NH * TS
        ssp = at("ssp", o_z + 16 * ZB, [P, 5, SW])
        sz = at("sz", o_h + 18432, [P, 5, SW])
        sl = at("sl", o_h + 18432 + 5120, [P, 5, SW])
        sw = at("sw", o_h + 18432 + 10240, [P, 5, SW])

        def pe_sample_stick(pe):
            pe.wait_ge(b_in, 32)
            pe.wait_ge(a_o, 8)
            for t in range(4):
                for i in range(PT):
                    mm = pe.transpose(PS[:, t, i * P:(i + 1) * P], kpt[:, i, t * P:(t + 1) * P], ident[:, :])
                mm.then_inc(b_kt, 1)
            pe.wait_ge(b_kr, 4)
            for kt in range(5):
                bank, n = 4 + 2 * (kt % 2), (P if kt < 4 else TS)
                if kt >= 2:
                    pe.wait_ge(b_na, kt - 1)
                for hh in range(NH):
                    e, p = hh % 2, hh // 2
                    r = slice(64 * e, 64 * e + 64)
                    key = kpT[r, p, kt * P:(kt + 1) * P] if kt < 4 else Z[r, EK + p, TP:NT]
                    mm = pe.matmul(PS[0:n, bank + e, p * TS:(p + 1) * TS], key, Z[r, EQ + p, TP:NT],
                                   start=True, stop=True)
                mm.then_inc(b_z, 1)
            pe.wait_ge(b_sp, 5)
            for kt in range(5):
                n = P if kt < 4 else TS
                for k2 in range(kt, 5):
                    m = P if k2 < 4 else TS
                    w = tri[0:m, 0:n] if k2 == kt else ones[0:m, 0:n]
                    mm = pe.matmul(PS[0:n, kt, 0:SW], w, ssp[0:m, k2, :], start=(k2 == kt), stop=(k2 == 4))
                mm.then_inc(b_s, 1)
            pe.wait_ge(b_w, 5)
            for hh in range(NH):
                e, p = hh % 2, hh // 2
                for kt in range(5):
                    m = P if kt < 4 else TS
                    v = vpt[:, kt, hh * HD:(hh + 1) * HD] if kt < 4 else vtok[0:TS, 8, hh * HD:(hh + 1) * HD]
                    mm = pe.matmul(PS[64 * e:64 * e + 64, 7, p * TS:(p + 1) * TS], v,
                                   sw[0:m, kt, e * P + p * TS:e * P + (p + 1) * TS], start=(kt == 0), stop=(kt == 4))
            mm.then_inc(b_pv, 1)

        def dve_sample_stick(dve, ch):
            for t in range(4):
                dve.wait_ge(b_kt, t + 1)
                dve.tensor_copy(kpT[:, t, :], PS[:, t, :]).then_inc(b_kr, 1)
            for kt in range(5):
                n = P if kt < 4 else TS
                dve.wait_ge(b_z, kt + 1)
                b0 = 4 + 2 * (kt % 2)
                ch.link(dve.tensor_scalar(sz[0:n, kt, :].rearrange("p (e c) -> p e c", e=2),
                                          PS[0:n, b0:b0 + 2, 0:P], HD ** -0.5, None, ALU.mult))
                if kt == 4:
                    for hh in range(NH):
                        x = sz[0:TS, kt, hh * TS:(hh + 1) * TS]
                        ins = dve.tensor_tensor(x, x, dneg[0:TS, 0:TS], ALU.add)
                        ch.link(ins)
                dve.scalar_tensor_tensor(sl[0:n, kt, :], sz[0:n, kt, :], -1.0, sz[0:n, kt, :], ALU.mult,
                                         ALU.min).then_inc(b_na, 1)
            dve.wait_ge(out_k, 32)
            for kt in range(5):
                n = P if kt < 4 else TS
                dve.wait_ge(b_l, kt + 1)
                dve.scalar_tensor_tensor(ssp[0:n, kt, :], sz[0:n, kt, :], 0.0, sl[0:n, kt, :],
                                         ALU.max, ALU.add).then_inc(b_sp, 1)
            for kt in range(5):
                n = P if kt < 4 else TS
                dve.wait_ge(b_s, kt + 1)
                dve.scalar_tensor_tensor(sw[0:n, kt, :], PS[0:n, kt, 0:SW], -1.0, sz[0:n, kt, :],
                                         ALU.mult, ALU.add).then_inc(b_t, 1)
            dve.wait_ge(b_pv, 1)
            dve.tensor_copy(Z[:, EQ:EQ + 4, TP:NT],
                            PS[:, 7, 0:P].rearrange("p (t q) -> p t q", t=4)).then_inc(att_a, 1)

        def act_sample_stick(act, ch):
            for kt in range(5):
                n = P if kt < 4 else TS
                act.wait_ge(b_na, kt + 1)
                x = sl[0:n, kt, :]
                ch.link(act.activation(x, x, ACT.Exp))
                act.activation(x, x, ACT.Ln, bias=1.0).then_inc(b_l, 1)
            for kt in range(5):
                n = P if kt < 4 else TS
                act.wait_ge(b_t, kt + 1)
                act.activation(sw[0:n, kt, :], sw[0:n, kt, :], ACT.Exp).then_inc(b_w, 1)

        r2 = lambda name, off, shape, dt=F32: at(name, o_h + off, shape, dt)
        Lb = r2("Lb", 0, [P, 3, D])
        pT = r2("pT", 12288, [P, 2, D])
        vtc = r2("vtc", 21504, [P, NTT, P])
        ktc = r2("ktc", 26112, [P, NTT, P])
        kptc = r2("kptc", 30720, [P, 2, PT, P])
        kpTc = r2("kpTc", 34816, [P, 2, PAST])
        vptc = r2("vptc", 38912, [P, PT, P])
        attq = r2("attq", 40960, [P, 512])
        m01 = r2("m01", 43008, [P, 2, 256])
        sel = r2("sel", 45056, [P, 3, D])
        cinp = r2("cinp", 45056, [P, 4, NT + 4])
        st = r2("st", 62016, [P, 4, 72])
        yc = r2("yc", 63168, [P, NT + 2])
        zslot = lambda name, s, shape: at(name, o_z + s * ZB, shape)
        rl = [zslot("rl0", 9, [P, D]), zslot("rl1", 10, [P, D])]
        kiD = zslot("kiD", 11, [P, NT])
        kipT = zslot("kipT", 12, [P, PAST])
        kitok = zslot("kitok", 13, [P, NTT, HD])
        kipt = zslot("kipt", 14, [P, PT, P])
        kic = zslot("kic", 15, [P, NTT, 68])
        kS = Z[:, 8, :]
        kip_in, kid_in = sem("kip_in"), sem("kid_in")
        i_tp, i_rd = sem("i_tp"), sem("i_rd")
        i_mm, i_relu, i_acc = sem("i_mm"), sem("i_relu"), sem("i_acc")
        ki_out, out_c = sem("ki_out"), sem("out_c")
        sel_done = sem("sel_done")
        c_tp, c_rd = sem("c_tp"), [sem("c_rd_dve"), sem("c_rd_act")]
        ks_in, cp_in, cst_in = sem("ks_in"), sem("cp_in"), sem("cst_in")
        cv_done = sem("cv_done")
        c_l, c_m, c_e, c_t, c_pt, c_pv = (sem(x) for x in ("c_logits", "c_max", "c_exp", "c_turned", "c_pt", "c_pv"))
        c_q, c_qt, c_at = sem("c_q"), sem("c_qt"), sem("c_at")
        ROWS = [P] * 6 + [TS]
        SC0 = [SCORE0[b] for b in range(2, 8)] + [SC_S]
        SCN = [P * (b + 1) for b in range(2, 8)] + [PAST + TS]

        def banks(b, n, m):
            return PS[0:m, b:b + 2, :].rearrange("p b n -> p (b n)")[:, 0:n]

        def act_z_evac(act, j0, s0, n, func):
            Zf = Z[:, :, :].rearrange("p s n -> p (s n)")
            with act.Fori(0, n // 2) as i:
                for t in range(2):
                    act.wait_ge(job_done, j0 + t + 1 + i * 2)
                    dst = Zf[:, bass.ds(i * (2 * NT) + (s0 + t) * NT, NT)]
                    act.activation(tri3(dst), psz(j0 + t), func).then_inc(set_free[(j0 + t) % 2], 1)

        def pe_odd(pe):
            pe.wait_ge(h_ready, 32)
            gemm_in_unit(pe, U_OIN, J_OI)
            gemm_in_unit(pe, U_OIN + 1, J_OI + 2, widths=(68,))
            pe.wait_ge(kip_in, 32)
            evacuated(pe, J_OI + 1)
            evacuated(pe, J_OI + 2)
            for i in range(PT):
                mm = pe.transpose(PS[:, 2, i * P:(i + 1) * P], kipt[:, i, :], ident[:, :])
            mm.then_inc(i_tp, 1)
            for i in range(NTT):
                c0, m = tok(i)
                mm = pe.transpose(PS[0:m, i // 7, (i % 7) * 68:(i % 7 + 1) * 68], Z[0:68, OKI, c0:c0 + m],
                                  ident[0:68, 0:68])
            mm.then_inc(i_tp, 1)
            pe.wait_ge(i_rd, 7)
            pe.wait_ge(kid_in, 16)
            for n in range(28):
                bi, hh = n // 4, n % 4
                if n >= 4:
                    pe.wait_ge(i_relu, n - 3)
                r = slice(64 * (hh % 2), 64 * (hh % 2) + 64)
                key = Z[0:64, OKI, :] if hh % 2 == 0 else kiD[64:128, :]
                b0 = 2 * (n % 4)
                if bi < 6:
                    b = bi + 2
                    q = Z[r, OQI + hh // 2, b * P:(b + 1) * P]
                    for c in range(0, SCN[bi], 512):
                        w = min(512, SCN[bi] - c)
                        mm = pe.matmul(PS[:, b0 + c // 512, 0:w], q, key[:, c:c + w], start=True, stop=True)
                else:
                    q = Z[r, OQI + hh // 2, TP:NT]
                    pe.matmul(PS[0:TS, b0, :], q, kipT[r, :], start=True, stop=True)
                    mm = pe.matmul(PS[0:TS, b0 + 1, 0:TS], q, key[:, TP:NT], start=True, stop=True)
                mm.then_inc(i_mm, 1)
            pe.wait_ge(i_relu, 28)
            with pe.Fori(0, 4) as i:
                for s in range(2):
                    gemm_in_unit(pe, U_OIN + 2 + s, J_OIN + 2 * s, du=i * 2, dj2=i * 2)
            gemm_in_unit(pe, U_OIN + 10, J_OIN + 16)
            pe_znorm(pe, O_NORMS, J_ON, 12)
            evacuated(pe, J_OOUT - 1)
            evacuated(pe, J_OOUT - 2)
            pe.wait_ge(zn, 17)
            pe.wait_ge(sel_done, 1)
            for n in range(6):
                s = OV if n < 3 else OK
                for t in range(3):
                    i = (n % 3) * 3 + t
                    c0, m = tok(i)
                    mm = pe.transpose(PS[0:m, n, t * P:(t + 1) * P], Z[:, s, c0:c0 + m], ident[:, :])
                mm.then_inc(c_tp, 1)
            pe.wait_ge(cp_in, 80)
            for n in range(2):
                for i in range(PT):
                    mm = pe.transpose(PS[:, 6 + n, i * P:(i + 1) * P], kptc[:, n, i, :], ident[:, :])
                mm.then_inc(c_tp, 1)
            pe.wait_ge(c_rd[0], 10)
            pe.wait_ge(ks_in, 32)
            def turn_out(b):
                m = P if b < 8 else TS
                pe.wait_ge(c_q, b + 1)
                if b >= 1:
                    pe.wait_ge(c_at, b)
                for k in range(4):
                    mm = pe.transpose(PS[:, 7, k * m:(k + 1) * m], attq[0:m, k * P:(k + 1) * P], ident[0:m, 0:m])
                mm.then_inc(c_qt, 1)

            for it in range(72 + 2):
                t = it
                if t < 72:
                    b, hh = t // 8, t % 8
                    g, e = hh // 4, hh % 2
                    r = slice(64 * e, 64 * e + 64)
                    keys = Z[r, OK, :] if g == e else kS[r, :]
                    if t >= 2:
                        pe.wait_ge(c_m, t - 1)
                    b0 = 2 * (t % 2)
                    if b < 8:
                        q = Z[r, OQ + hh // 2, b * P:(b + 1) * P]
                        for c in range(0, (b + 1) * P, 512):
                            w = min(512, (b + 1) * P - c)
                            mm = pe.matmul(PS[:, b0 + c // 512, 0:w], q, keys[:, c:c + w], start=True, stop=True)
                    else:
                        q = Z[r, OQ + hh // 2, TP:NT]
                        pe.matmul(PS[0:TS, b0, :], q, kpTc[r, 0 if g == e else 1, :], start=True, stop=True)
                        mm = pe.matmul(PS[0:TS, b0 + 1, 0:TS], q, keys[:, TP:NT], start=True, stop=True)
                    mm.then_inc(c_l, 1)
                t = it - 1
                if 0 <= t < 72:
                    b, hh = t // 8, t % 8
                    pe.wait_ge(c_e, t + 1)
                    if t >= 1:
                        pe.wait_ge(c_pt, t)
                    if b < 8:
                        for kt in range(b + 1):
                            mm = pe.transpose(PS[:, 4 + kt // 4, (kt % 4) * P:(kt % 4 + 1) * P],
                                              Lb[:, t % 3, kt * P:(kt + 1) * P], ident[:, :])
                    else:
                        for kt in range(5):
                            w = P if kt < 4 else TS
                            mm = pe.transpose(PS[0:w, 4, kt * TS:(kt + 1) * TS],
                                              Lb[0:TS, t % 3, kt * P:kt * P + w], ident[0:TS, 0:TS])
                    mm.then_inc(c_t, 1)
                t = it - 2
                if 0 <= t < 72:
                    b, hh = t // 8, t % 8
                    g = hh // 4
                    pe.wait_ge(c_pt, t + 1)
                    if hh == 0 and b >= 1:
                        pe.wait_ge(c_q, b)
                    o = PS[0:(P if b < 8 else TS), 6, hh * HD:(hh + 1) * HD]
                    n = b + 1 if b < 8 else 5
                    for kt in range(n):
                        if b < 8:
                            w, v = pT[:, t % 2, kt * P:(kt + 1) * P], vtc[:, kt, g * HD:(g + 1) * HD]
                        elif kt < 4:
                            w, v = pT[:, t % 2, kt * TS:(kt + 1) * TS], vptc[:, kt, g * HD:(g + 1) * HD]
                        else:
                            w, v = pT[0:TS, t % 2, kt * TS:(kt + 1) * TS], vtc[0:TS, 8, g * HD:(g + 1) * HD]
                        mm = pe.matmul(o, w, v, start=(kt == 0), stop=(kt == n - 1))
                    mm.then_inc(c_pv, 1)
                if it % 8 == 3 and it >= 8:
                    turn_out(it // 8 - 1)
            turn_out(8)
            pe.wait_ge(c_at, 9)
            pe_outproj(pe, U_OOUT, J_OOUT, 4)

        def act_odd(act, ch):
            for t in range(2):
                act.wait_ge(job_done, J_OI + t + 1)
                act.activation(tri3(Z[:, OQI + t, :]), psz(J_OI + t), ACT.Copy).then_inc(set_free[(J_OI + t) % 2], 1)
            act.wait_ge(job_done, J_OI + 3)
            act.activation(tri3(Z[0:68, OKI, :]), psz(J_OI + 2)[0:68], ACT.Copy)\
               .then_inc(set_free[(J_OI + 2) % 2], 1)
            for n in range(28):
                bi = n // 4
                act.wait_ge(i_mm, n + 1)
                if n >= 2:
                    act.wait_ge(i_acc, n - 1)
                m = ROWS[bi]
                act.activation(rl[n % 2][0:m, 0:SCN[bi]], banks(2 * (n % 4), SCN[bi], m), ACT.Relu,
                               scale=HD ** -0.5).then_inc(i_relu, 1)
            act.wait_ge(i_acc, 28)
            act.wait_ge(ki_out, 32)
            act_z_evac(act, J_OIN, OQ, 6, ACT.Copy)
            act_z_evac(act, J_OIN + 6, OB, 12, ACT.Copy)
            act_znorm(act, O_NORMS, J_ON, 12, J_ON)
            for t in range(72):
                b, hh = t // 8, t % 8
                m, n = (P, (b + 1) * P) if b < 8 else (TS, PAST + TS)
                act.wait_ge(c_m, t + 1)
                act.activation(Lb[0:m, t % 3, 0:n], Lb[0:m, t % 3, 0:n], ACT.Exp, bias=st[0:m, 1, t:t + 1],
                               accum_out=st[0:m, 2, t:t + 1]).then_inc(c_e, 1)
                if t >= 1:
                    act_pt(act, t - 1)
            act_pt(act, 71)
            act_mix(act, 4, [0, 1, 2, 3, 9, 10, 11, 12], c_at, 9, out_c, 128)

        def act_pt(act, t):
            b = t // 8
            act.wait_ge(c_t, t + 1)
            if t >= 2:
                act.wait_ge(c_pv, t - 1)
            if b < 8:
                n = (b + 1) * P
                act.activation(pT[:, t % 2, 0:n], banks(4, n, P), ACT.Copy).then_inc(c_pt, 1)
            else:
                act.activation(pT[0:TS, t % 2, P:P + TS], PS[0:TS, 4, P:P + TS], ACT.Copy).then_inc(act_step, 1)
                act.activation(pT[:, t % 2, 0:P], PS[:, 4, 0:P], ACT.Copy).then_inc(c_pt, 1)

        def dve_odd(dve, ch):
            dve.wait_ge(i_tp, 1)
            dve.tensor_copy(kipT[:, :], PS[:, 2, :]).then_inc(i_rd, 1)
            dve.wait_ge(i_tp, 2)
            for i0, n, m, b in ((0, 7, P, 0), (7, 1, P, 1), (8, 1, TS, 1)):
                c = (i0 - 7 * b) * 68
                src = PS[0:m, b, c:c + n * 68].rearrange("p (i d) -> p i d", d=68)
                dve.tensor_copy(kitok[0:m, i0:i0 + n, :], src[:, :, 0:HD]).then_inc(i_rd, 1)
                dve.tensor_scalar(wi[0:m, i0:i0 + n, :], src[:, :, HD:68], 4 ** -0.5, None, ALU.mult).then_inc(i_rd, 1)
            dve.wait_ge(i_rd, 7)
            for n in range(28):
                bi, hh = n // 4, n % 4
                m = ROWS[bi]
                tile = bi + 2 if bi < 6 else 8
                s = score[0:m, SC0[bi]:SC0[bi] + SCN[bi]]
                x, w = rl[n % 2][0:m, 0:SCN[bi]], wi[0:m, tile, hh:hh + 1]
                dve.wait_ge(i_relu, n + 1)
                if hh == 0:
                    dve.tensor_scalar(s, x, w, None, ALU.mult).then_inc(i_acc, 1)
                else:
                    dve.wait_ge(i_acc, n)
                    dve.scalar_tensor_tensor(s, x, w, s, ALU.mult, ALU.add).then_inc(i_acc, 1)
                if hh == 3 and bi < 6:
                    dve.wait_ge(i_acc, n + 1)
                    ch.link(dve.memset(score[0:64, SC0[bi] + SCN[bi] - 64:SC0[bi] + SCN[bi]], NEG))
            KEY, BIT, CAND, MSK, CNT, OKF, OKI_, KV, THR, GT = range(10)
            f = lambda r: bs_[:, r, 0:7]
            u = lambda r: bs_[:, r, 0:7].bitcast(I32)
            dve.wait_ge(i_acc, 28)
            ch.link(dve.memset(bs_[:, :, :], 0.0))
            ch.link(dve.tensor_scalar(u(BIT), u(KEY), -2147483648, None, ALU.bitwise_or))
            ch.link(dve.memset(bs_[:, KV, 0:6], float(TOPK)))
            ch.link(dve.memset(bs_[:, KV, 6:7], float(TOPK_S)))

            def to_float(src):
                ch.link(dve.tensor_scalar(u(MSK), u(src), 31, -1, ALU.arith_shift_right, ALU.bitwise_xor))
                ch.link(dve.scalar_tensor_tensor(u(THR), u(MSK), -2147483648, u(src), ALU.bitwise_or,
                                                 ALU.bitwise_xor))

            with dve.Fori(0, 32) as i:
                ch.begin(i, 15)
                ch.link(dve.tensor_tensor(u(CAND), u(KEY), u(BIT), ALU.bitwise_or))
                to_float(CAND)
                for bi in range(7):
                    m = ROWS[bi]
                    ins = dve.tensor_scalar(banks(6, SCN[bi], m), score[0:m, SC0[bi]:SC0[bi] + SCN[bi]],
                                            bs_[0:m, THR, bi:bi + 1], 0.0, ALU.is_ge, ALU.add,
                                            accum_out=bs_[0:m, CNT, bi:bi + 1])
                    ch.link(ins)
                ch.link(dve.tensor_tensor(f(OKF), f(CNT), f(KV), ALU.is_ge))
                ch.link(dve.tensor_scalar(u(OKI_), f(OKF), -1.0, None, ALU.mult))
                ch.link(dve.tensor_tensor(u(OKI_), u(OKI_), u(BIT), ALU.bitwise_and))
                ch.link(dve.tensor_tensor(u(KEY), u(KEY), u(OKI_), ALU.bitwise_or))
                ch.link(dve.tensor_scalar(u(BIT), u(BIT), 1, None, ALU.logical_shift_right))
            ch.end(32)
            to_float(KEY)
            dve.wait_ge(job_done, J_ON)
            for bi in range(7):
                m, n = ROWS[bi], SCN[bi]
                s = score[0:m, SC0[bi]:SC0[bi] + n]
                gt, eq, rank = (sel[0:m, r, 0:n] for r in range(3))
                thr = bs_[0:m, THR, bi:bi + 1]
                ch.link(dve.tensor_scalar(gt, s, thr, 0.0, ALU.is_gt, ALU.add, accum_out=bs_[0:m, GT, bi:bi + 1]))
                ch.link(dve.tensor_tensor(bs_[0:m, GT, bi:bi + 1], bs_[0:m, KV, bi:bi + 1],
                                          bs_[0:m, GT, bi:bi + 1], ALU.subtract))
                ch.link(dve.tensor_scalar(eq, s, thr, None, ALU.is_equal))
                ch.link(dve.tensor_tensor_scan(rank, eq, eq, 0.0, ALU.add, ALU.max))
                ch.link(dve.scalar_tensor_tensor(eq, rank, bs_[0:m, GT, bi:bi + 1], eq, ALU.is_le, ALU.mult))
                ch.link(dve.tensor_tensor(gt, gt, eq, ALU.add))
                ch.link(dve.tensor_scalar(s, gt, -1.0, BIG, ALU.add, ALU.mult))
            ch.link(dve.memset(m01[:, :, :], 0.0))
            ch.link(dve.memset(m01[0:64, 0, 64:128], NEG))
            dve.memset(m01[0:64, 1, 192:256], NEG).then_inc(sel_done, 1)
            dve.wait_ge(sel_done, 1)
            dve_znorm(dve, ch, O_NORMS, J_ON)
            for n in range(6):
                x = vtc if n < 3 else ktc
                dve.wait_ge(c_tp, n + 1)
                i = (n % 3) * 3
                if n % 3 < 2:
                    dve.tensor_copy(x[:, i:i + 3, :], PS[:, n, 0:3 * P].rearrange("p (i d) -> p i d", i=3)).then_inc(c_rd[0], 1)
                else:
                    dve.tensor_copy(x[:, 6:8, :], PS[:, n, 0:2 * P].rearrange("p (i d) -> p i d", i=2)).then_inc(c_rd[0], 1)
                    dve.tensor_copy(x[0:TS, 8, :], PS[0:TS, n, 2 * P:3 * P]).then_inc(c_rd[0], 1)
            for n in range(2):
                dve.wait_ge(c_tp, 7 + n)
                dve.tensor_copy(kpTc[:, n, :], PS[:, 6 + n, :]).then_inc(c_rd[0], 1)
            dve.wait_ge(cst_in, 32)
            prod = lambda a, b: (Z[:, OC:OC + 4, a:b], Z[:, OH:OH + 4, a:b])
            ch.link(dve.memset(cinp[:, :, 0:2], 0.0))
            a, b = prod(0, TP)
            dve.tensor_tensor(cinp[:, :, 2:2 + TP], a, b, ALU.mult).then_inc(cv_done, 1)
            a, b = prod(TP, NT)
            dve.tensor_tensor(cinp[:, :, TP + 4:NT + 4], a, b, ALU.mult).then_inc(cv_done, 1)
            dve.wait_ge(cv_done, 2)
            for k in range(4):
                x = [cinp[:, k, j:j + NT + 2] for j in range(3)]
                w = [gv[:, G_CW + 4 * j + k:G_CW + 4 * j + k + 1] for j in range(3)]
                ch.link(dve.tensor_scalar(yc[:, :], x[0], w[0], None, ALU.mult))
                for j in (1, 2):
                    ch.link(dve.scalar_tensor_tensor(yc[:, :], x[j], w[j], yc[:, :], ALU.mult, ALU.add))
                for z0, z1, y0 in ((0, TP, 0), (TP, NT, TP + 2)):
                    z = Z[:, OB + k, z0:z1]
                    ins = dve.tensor_tensor(z, z, yc[:, y0:y0 + z1 - z0], ALU.mult)
                    ch.link(ins)
            for t in range(72):
                b, hh = t // 8, t % 8
                m, n = (P, (b + 1) * P) if b < 8 else (TS, PAST + TS)
                if b < 2:
                    mask = m01[:, b, 0:n]
                else:
                    mask = score[0:m, SC0[b - 2]:SC0[b - 2] + n]
                dve.wait_ge(c_l, t + 1)
                if t >= 3:
                    dve.wait_ge(c_t, t - 2)
                ch.link(dve.tensor_tensor_reduce(Lb[0:m, t % 3, 0:n], banks(2 * (t % 2), n, m), mask, HD ** -0.5,
                                                 -3e38, ALU.add, ALU.max, st[0:m, 0, t:t + 1]))
                dve.tensor_scalar(st[0:m, 1, t:t + 1], st[0:m, 0, t:t + 1], -1.0, None, ALU.mult).then_inc(c_m, 1)
                if t >= 8 and hh == 2:
                    dve_block_norm(dve, ch, b - 1)
                if t >= 8 and hh == 4:
                    dve_block_out(dve, b - 1)
            dve_block_norm(dve, ch, 8)
            dve_block_out(dve, 8)
            dve_mix(dve, 4, [0, 1, 2, 3, 9, 10, 11, 12])
            dve_outproj(dve, J_OOUT, 2)

        def dve_block_norm(dve, ch, b):
            m = P if b < 8 else TS
            dve.wait_ge(c_pv, 8 * b + 8)
            dve.wait_ge(c_e, 8 * b + 8)
            r = st[0:m, 3, 8 * b:8 * b + 8]
            ch.link(dve.reciprocal(r, st[0:m, 2, 8 * b:8 * b + 8]))
            if b >= 1:
                dve.wait_ge(c_qt, b)
            dve.tensor_tensor(attq[0:m, :].rearrange("p (h d) -> p h d", h=8),
                              PS[0:m, 6, :].rearrange("p (h d) -> p h d", h=8),
                              r.unsqueeze(2).to_broadcast([m, 8, HD]), ALU.mult).then_inc(c_q, 1)

        def dve_block_out(dve, b):
            m = P if b < 8 else TS
            c0 = b * P
            dve.wait_ge(c_qt, b + 1)
            dve.tensor_copy(Z[:, OQ:OQ + 4, c0:c0 + m],
                            PS[:, 7, 0:4 * m].rearrange("p (k q) -> p k q", k=4)).then_inc(c_at, 1)

        def sp_odd(sp_, weights):
            w = cols(dram["w_in_odd"][0])

            def unit(n):
                c, width = ODD_UNITS[n]
                weights(U_OIN + n, w[:, :, c:c + width], width)

            unit(0)
            unit(1)
            ki = dram["cache_c_kidx"][0, 0].rearrange("(i p) d -> p i d", p=P)
            sp_.wait_ge(job_done, J_N2 + 1)
            for e in range(2):
                sp_.dma_start(kipt[:, :, 64 * e:64 * e + 64], ki).then_inc(kip_in, 16)
            evacuated(sp_, J_OI + 2)
            sp_.dma_start(kiD[64:128, :], Z[0:64, OKI, :]).then_inc(kid_in, 16)
            unit(2)
            unit(3)
            sp_.wait_ge(i_rd, 7)
            sp_.dma_start(dram["new_c_kidx_prompt"][0, 0].rearrange("(i p) d -> p i d", p=P),
                          kitok[:, 0:8, :]).then_inc(ki_out, 16)
            sp_.dma_start(dram["new_c_kidx_sample"][0, 0], kitok[0:TS, 8, :]).then_inc(ki_out, 16)
            for n in range(4, 11):
                unit(n)
            for n in range(2):
                weights(U_OOUT + n, cols(dram["w_out_odd"][0])[:, :, n * 256:(n + 1) * 256])
            sp_.wait_ge(job_done, J_ON)
            kc = dram["cache_c_k"][0, 0].rearrange("(i p) g d -> g p i d", p=P)
            for n in range(2):
                for g in range(2):
                    e = g if n == 0 else 1 - g
                    sp_.dma_start(kptc[:, n, :, 64 * e:64 * e + 64], kc[g]).then_inc(cp_in, 16)
            sp_.dma_start(vptc[:, :, :], dram["cache_c_v"][0, 0].rearrange("(i p) g d -> p i (g d)", p=P)).then_inc(cp_in, 16)
            sp_.wait_ge(sel_done, 1)
            for j in range(2):
                sp_.dma_start(cinp[:, :, TP + 2 + j], dram["state_d_conv"][0, 0, j].rearrange("(k p) -> p k", p=P),
                              allow_slow_non_contiguous=True).then_inc(cst_in, 16)
            sp_.wait_ge(zn, 17)
            sp_.dma_start(kS[64:128, :], Z[0:64, OK, :]).then_inc(ks_in, 16)
            sp_.dma_start(kS[0:64, :], Z[64:128, OK, :]).then_inc(ks_in, 16)
            sp_.wait_ge(c_rd[0], 8)
            for name, x in (("new_c_v", vtc), ("new_c_k", ktc)):
                sp_.dma_start(dram[name + "_prompt"][0, 0].rearrange("(i p) g d -> p i (g d)", p=P),
                              x[:, 0:8, :]).then_inc(out_c, 16)
                sp_.dma_start(dram[name + "_sample"][0, 0].rearrange("t g d -> t (g d)"),
                              x[0:TS, 8, :]).then_inc(out_c, 16)
            sp_.wait_ge(cv_done, 2)
            for name, c in (("prompt", TP), ("sample", NT + 2)):
                for j in range(2):
                    sp_.dma_start(dram["new_d_conv_" + name][0, 0, j].rearrange("(k p) -> p k", p=P),
                                  cinp[:, :, c + j], allow_slow_non_contiguous=True).then_inc(out_c, 16)
            for n in range(2, 4):
                weights(U_OOUT + n, cols(dram["w_out_odd"][0])[:, :, n * 256:(n + 1) * 256])

        out_vb = sem("out_vb")
        y_tp = sem("y_tp")
        y_rd = [sem("y_dve"), sem("y_act")]
        out_k, out_v = sem("out_k"), sem("out_v")

        block = ctx.enter_context(nc.Block())
        cols = lambda w: w.rearrange("(k p) n -> p k n", p=P)
        rows = lambda w: w.rearrange("(r p) n -> p r n", p=P)
        stage_in = [stage[:, s, :].rearrange("p (k n) -> p k n", k=KT) for s in range(2)]
        stage_dn = [stage[:, s, :].rearrange("p (k n) -> p k n", k=2) for s in range(2)]

        @block.sync
        def _(sp_):
            xp = dram["x_prompt"][0].rearrange("(i p) d -> i p d", p=P)
            for i in range(NTT):
                src = xp[i] if i < 8 else dram["x_sample"][0]
                sp_.dma_start(xtok[0:tok(i)[1], i, :], src).then_inc(x_in[i], 16)

            def weights(u, src, width=256, du=0):
                s = u % 2
                if u >= 2:
                    sp_.wait_ge(w_split, u - 1 + du)
                dst = stage_in[s][:, :, 0:width] if src.shape[1] == KT else stage_dn[s]
                sp_.dma_start(dst, src).then_inc(w_stage[s], 16)

            def in_units(u0, w, n):
                for s in range(2):
                    weights(u0 + s, w[:, :, s * 256:(s + 1) * 256])
                with sp_.Fori(1, n // 2) as i:
                    for s in range(2):
                        weights(u0 + 2 + s, w[:, :, bass.ds(i * 512 + s * 256, 256)], du=(i - 1) * 2)

            def ffn_units(u0, w1, w2):
                weights(u0, w1[:, :, 0:256])
                with sp_.Fori(0, NCHUNK - 1) as c:
                    weights(u0 + 1, w1[:, :, bass.ds(c * 256 + 256, 256)], du=c * 2)
                    weights(u0 + 2, w2[:, bass.ds(c * 2, 2), :], du=c * 2)
                weights(u0 + 31, w2[:, 30:32, :])

            in_units(U_EIN, cols(dram["w_in_even"][0]), 10)
            sp_.dma_start(wsb[:, :, :], dram["ws_b"][0].rearrange("g p q -> p g q")).then_inc(ws_in, 16)
            sp_.dma_start(bsr[:, :], dram["bs_b"].rearrange("a g p -> a (g p)")).then_inc(ws_in, 16)
            weights(U_EOUT, cols(dram["w_out_even"][0])[:, :, 0:256])
            weights(U_EOUT + 1, cols(dram["w_out_even"][0])[:, :, 256:512])
            sp_.wait_ge(zn, 12)
            sp_.dma_start(kpt[:, :, :], dram["cache_a_k"][0, 0].rearrange("(i p) h d -> p i (h d)", p=P)).then_inc(b_in, 16)
            sp_.dma_start(vpt[:, :, :], dram["cache_a_v"][0, 0].rearrange("(i p) h d -> p i (h d)", p=P)).then_inc(b_in, 16)
            sp_.wait_ge(turn_rd[0], 14)
            sp_.wait_ge(turn_rd[1], 13)
            for name, x in (("new_a_v", vtok), ("new_a_k", ktok)):
                so = out_k if x is ktok else out_v
                sp_.dma_start(dram[name + "_prompt"][0, 0].rearrange("(i p) h d -> p i (h d)", p=P),
                              x[:, 0:8, :]).then_inc(so, 16)
                sp_.dma_start(dram[name + "_sample"][0, 0].rearrange("t h d -> t (h d)"),
                              x[0:TS, 8, :]).then_inc(so, 16)
            sp_.dma_start(dram["new_b_v_sample"][0, 0], vbtok[0:TS, 8, :]).then_inc(out_vb, 16)
            weights(U_EOUT + 2, cols(dram["w_out_even"][0])[:, :, 512:768])
            weights(U_EOUT + 3, cols(dram["w_out_even"][0])[:, :, 768:1024])
            ffn_units(U_F0, cols(dram["w_ffn1"][0]), rows(dram["w_ffn2"][0]))
            sp_odd(sp_, weights)
            ffn_units(U_F1, cols(dram["w_ffn1"][1]), rows(dram["w_ffn2"][1]))
            yp = dram["y_prompt"][0].rearrange("(i p) d -> i p d", p=P)
            for i in range(NTT):
                sp_.wait_ge(y_rd[i % 2], i // 2 + 1)
                out_start(sp_, yp[i] if i < 8 else dram["y_sample"][0], xtok[0:tok(i)[1], i, :])
            sp_.wait_ge(out_k, 32)
            sp_.wait_ge(out_v, 32)
            sp_.wait_ge(out_vb, 16)
            sp_.wait_ge(ki_out, 32)
            sp_.wait_ge(out_c, 128)
            sp_.wait_ge(out_dma, 16 * outs[0])

        @block.gpsimd
        def _(pool):
            pool.memset(ident[:, :], 0.0).then_inc(pool_step, 1)
            pool.memset(ones[:, :], 1.0).then_inc(pool_step, 1)
            pool.memset(blk[:, :], 0.0).then_inc(pool_step, 1)
            pool.memset(dneg[:, :], NEG).then_inc(pool_step, 1)
            pool.memset(eps[:, :], EPS).then_inc(consts, 1)
            pool.wait_ge(pool_step, 4)
            pool.affine_select(out=ident[:, :], in_=ident[:, :], compare_op=ALU.not_equal, fill=1.0, base=0,
                               pattern=[[-1, P]], channel_multiplier=1).then_inc(consts, 1)
            pool.affine_select(out=tri[:, :], in_=ones[:, :], compare_op=ALU.is_ge, fill=0.0, base=0,
                               pattern=[[-1, P]], channel_multiplier=1).then_inc(consts, 1)
            pool.affine_select(out=ctri[:, :], in_=ones[:, :], compare_op=ALU.is_gt, fill=0.0, base=0,
                               pattern=[[1, P]], channel_multiplier=-1).then_inc(consts, 1)
            pool.affine_select(out=dneg[:, :], in_=dneg[:, :], compare_op=ALU.is_ge, fill=0.0, base=0,
                               pattern=[[-1, P]], channel_multiplier=1).then_inc(consts, 1)
            pool.wait_ge(consts, 5)
            pool.memset(blk[0:64, 0:64], 1.0).then_inc(consts, 1)
            pool.wait_ge(consts, 6)
            pool.memset(blk[64:128, 64:128], 1.0).then_inc(consts, 1)

            def last_job(u):
                for u0, j0, n in ((U_EIN, J_EIN, 10), (U_EOUT, J_EOUT, 4), (U_OOUT, J_OOUT, 4)):
                    if u0 <= u < u0 + n:
                        return j0 + 2 * (u - u0) + 1
                if U_OIN <= u < U_OOUT:
                    n = u - U_OIN
                    return J_OI + 2 * n + 1 if n == 0 else J_OI + 2 * n
                u0, j0 = (U_F0, J_F0) if u < U_OIN else (U_F1, J_F1)
                n = u - u0
                if n == 0:
                    return j0 + 1
                if n == 31:
                    return j0 + 159
                return j0 + 2 + 10 * ((n - 1) // 2) + (1 if n % 2 else 9)

            def split(u, du=0, ds=0, dj=0):
                s = u % 2
                pool.wait_ge(w_stage[s], 16 * (u // 2 + 1) + ds)
                if u >= 2:
                    pool.wait_ge(job_done, last_job(u - 2) + 1 + dj)
                pool.tensor_tensor(w_sp[:, s, 0, :], stage[:, s, :], ones[:, 0:1].to_broadcast([P, UN]),
                                   ALU.mult).then_inc(w_hi_done, 1)
                pool.wait_ge(w_hi_done, u + 1 + du)
                pool.tensor_tensor(w_sp[:, s, 1, :], stage[:, s, :], w_sp[:, s, 0, :].bitcast(F32),
                                   ALU.subtract).then_inc(w_split, 1)

            def split_ffn(u0):
                for n in range(3):
                    split(u0 + n)
                with pool.Fori(0, NCHUNK - 2) as i:
                    for n in (3, 4):
                        split(u0 + n, du=i * 2, ds=i * 16, dj=i * 10)
                split(u0 + 31)

            pool.wait_ge(consts, 7)
            split(0)
            split(1)
            with pool.Fori(0, 4) as i:
                for u in (2, 3):
                    split(u, du=i * 2, ds=i * 16, dj=i * 4)
            for u in range(U_EOUT, U_F0):
                split(u)
            split_ffn(U_F0)
            for u in range(U_OIN, U_F1):
                split(u)
            split_ffn(U_F1)

        @block.scalar
        def _(act):
            ch = Chain(act, act_step)
            nv = 0
            loads = [(gv[:, G_MIX:G_MIX + 16], dram["norm_mix_g"].rearrange("l (k p) -> p (l k)", p=P)),
                     (gv[:, G_FFN:G_FFN + 16], dram["norm_ffn_g"].rearrange("l (k p) -> p (l k)", p=P)),
                     (gv[:, G_VB:G_VB + 4], dram["g_b"].rearrange("a (k p) -> p (a k)", p=P)),
                     (gv[:, G_CW:G_CW + 12], dram["conv_w_d"][0].rearrange("j (k p) -> p (j k)", p=P))]
            for c, name in ((G_QA, "gq_a"), (G_KA, "gk_a"), (G_QC, "gq_c"), (G_KC, "gk_c")):
                for e in range(2):
                    loads.append((gv[64 * e:64 * e + 64, c:c + 1], dram[name].rearrange("a d -> d a")))
            for dst, src in loads:
                act.dma_start(dst, src, allow_slow_non_contiguous=True).then_inc(vecs, 16)
            act.wait_ge(consts, 7)
            act_norm(act, 0)
            act.wait_ge(spilled, 16)
            act_z_evac(act, J_EIN, EQ, 12, ACT.Copy)
            act_z_evac(act, J_EIN + 12, EU, 8, ACT.Gelu_apprx_tanh)
            act_znorm(act, E_NORMS, J_EN, 0, J_EN)
            read_even_turns(act, 1)
            act.preload_act_table_set("natural_log_exp_and_others")
            act_stick(act, ch)
            act_sample_stick(act, ch)
            act_mix(act, 1, [0, 1, 2, 3, 12, 13, 14, 15], att_a, 1, out_v, 32)
            act_norm(act, 1)
            act_ffn(act, ch, J_F0, 0)
            act_norm(act, 2)
            act.wait_ge(spilled, 32)
            act_odd(act, ch)
            act_norm(act, 3)
            act_ffn(act, ch, J_F1, 32)
            for i in range(1, NTT, 2):
                act.wait_ge(y_tp, i + 1)
                act.activation(xtok[0:tok(i)[1], i, :].rearrange("p (b n) -> p b n", b=2),
                               PS[0:tok(i)[1], 2 * (i % 4):2 * (i % 4) + 2, :], ACT.Copy).then_inc(y_rd[1], 1)

        @block.vector
        def _(dve):
            ch = Chain(dve, dve_step)
            for i in range(NTT):
                c0, m = tok(i)
                dve.wait_ge(x_tp, i + 1)
                b = 2 * (i % 4)
                dve.tensor_copy(xT[:, :, c0:c0 + m], PS[:, b:b + 2, :].rearrange("p b (k n) -> p (b k) n", k=4)[:, :, 0:m])\
                   .then_inc(xT_ready, 1)
            dve.wait_ge(vecs, 16 * 12)
            dve_norm(dve, ch, 0)
            dve_znorm(dve, ch, E_NORMS, J_EN)
            read_even_turns(dve, 0)
            dve_spatial(dve, ch)
            dve.wait_ge(out_vb, 16)
            dve_stick(dve, ch)
            dve_sample_stick(dve, ch)
            dve_mix(dve, 1, [0, 1, 2, 3, 12, 13, 14, 15])
            dve_outproj(dve, J_EOUT, 1)
            dve_norm(dve, ch, 1)
            dve_ffn(dve, ch, J_F0, 0)
            dve_norm(dve, ch, 2)
            dve_odd(dve, ch)
            dve_norm(dve, ch, 3)
            dve_ffn(dve, ch, J_F1, 32)
            for i in range(0, NTT, 2):
                dve.wait_ge(y_tp, i + 1)
                dve.tensor_copy(xtok[0:tok(i)[1], i, :].rearrange("p (b n) -> p b n", b=2),
                                PS[0:tok(i)[1], 2 * (i % 4):2 * (i % 4) + 2, :]).then_inc(y_rd[0], 1)

        @block.tensor
        def _(pe):
            pe.wait_ge(consts, 7)
            for i in range(NTT):
                c0, m = tok(i)
                pe.wait_ge(x_in[i], 16)
                if i >= 4:
                    pe.wait_ge(xT_ready, i - 3)
                for k in range(KT):
                    mm = pe.transpose(PS[:, 2 * (i % 4) + k // 4, (k % 4) * P:(k % 4) * P + m],
                                      xtok[0:m, i, k * P:(k + 1) * P], ident[0:m, 0:m])
                mm.then_inc(x_tp, 1)
            pe.wait_ge(xT_ready, NTT)
            pe_norm(pe, 0)
            pe.wait_ge(h_ready, 8)
            with pe.Fori(0, 5) as i:
                for s in range(2):
                    gemm_in_unit(pe, U_EIN + s, J_EIN + 2 * s, du=i * 2, dj2=i * 2)
            pe_znorm(pe, E_NORMS, J_EN, 0)
            evacuated(pe, J_EOUT - 1)
            evacuated(pe, J_EOUT - 2)
            pe_even_turns(pe)
            pe_spatial(pe)
            pe_stick(pe)
            pe_sample_stick(pe)
            pe.wait_ge(att_a, 1)
            pe_outproj(pe, U_EOUT, J_EOUT, 1)
            pe_norm(pe, 1)
            pe_ffn(pe, U_F0, J_F0, 2, 0)
            pe_norm(pe, 2)
            pe_odd(pe)
            pe_norm(pe, 3)
            pe_ffn(pe, U_F1, J_F1, 5, 32)
            for m in range(KT):
                x_tile_ready(pe, 4, m)
            for i in range(NTT):
                c0, m = tok(i)
                if i >= 4:
                    pe.wait_ge(y_rd[i % 2], (i - 4) // 2 + 1)
                for k in range(KT):
                    mm = pe.transpose(PS[0:m, 2 * (i % 4) + k // 4, (k % 4) * P:(k % 4 + 1) * P],
                                      xT[:, k, c0:c0 + m], ident[:, :])
                mm.then_inc(y_tp, 1)


_INS = ["x_prompt", "x_sample", "cache_a_k", "cache_a_v", "cache_c_k", "cache_c_v", "cache_c_kidx", "state_d_conv",
        "norm_mix_g", "norm_ffn_g", "w_in_even", "gq_a", "gk_a", "g_b", "ws_b", "bs_b", "w_out_even",
        "w_in_odd", "gq_c", "gk_c", "conv_w_d", "w_out_odd", "w_ffn1", "w_ffn2"]
_OUTS = [("y_prompt", (1, TP, D)), ("y_sample", (1, TS, D)),
         ("new_a_k_prompt", (1, 1, TP, NH, HD)), ("new_a_v_prompt", (1, 1, TP, NH, HD)),
         ("new_a_k_sample", (1, 1, TS, NH, HD)), ("new_a_v_sample", (1, 1, TS, NH, HD)),
         ("new_b_v_sample", (1, 1, TS, 512)),
         ("new_c_k_prompt", (1, 1, TP, 2, HD)), ("new_c_v_prompt", (1, 1, TP, 2, HD)),
         ("new_c_kidx_prompt", (1, 1, TP, HD)),
         ("new_c_k_sample", (1, 1, TS, 2, HD)), ("new_c_v_sample", (1, 1, TS, 2, HD)),
         ("new_c_kidx_sample", (1, 1, TS, HD)),
         ("new_d_conv_prompt", (1, 1, 2, 512)), ("new_d_conv_sample", (1, 1, 2, 512))]


def kernel(**inputs):
    import numpy as _np
    import concourse.bacc as _bacc
    from concourse import mybir as _mybir
    from concourse.bass_utils import run_bass_kernel_spmd as _run

    nc = _bacc.Bacc("TRN2", target_bir_lowering=False, num_devices=1, dynamic_dma_scratch_size=1024)
    arrays, dram = {}, {}
    for name in _INS:
        a = _np.ascontiguousarray(inputs[name])
        arrays[f"in_{name}"] = a
        dram[name] = nc.dram_tensor(f"in_{name}", a.shape, _mybir.dt.from_np(a.dtype), kind="ExternalInput").ap()
    for name, shape in _OUTS:
        dram[name] = nc.dram_tensor(f"out_{name}", shape, _mybir.dt.float32, kind="ExternalOutput").ap()
    build_encoder(nc, dram)
    r = _run(nc, [arrays], core_ids=[0])
    return tuple(r.results[0][f"out_{name}"] for name, _ in _OUTS)
```
